# Optimizing a Trainium2 kernel written in Bass

```python
import jax, jax.numpy as jnp
from jax import lax
import numpy as np

D_MODEL = 2048
BATCH = 1
SEQ = 512
DEPTH = 2

PLE_DIM = 256
N_HEADS = 16
Q_LORA = 512
KV_LORA = 512
QK_NOPE = 128
QK_ROPE = 64
QK_HEAD = QK_NOPE + QK_ROPE
V_HEAD = 128
ATT_WIDTH = N_HEADS * V_HEAD
ROPE_THETA = 10000.0
Q_BLOCK = 128
CONV_WIDTH = D_MODEL
CONV_K = 3
CONV_GROUPS = 16
N_MIXERS = 2
N_MLA = (DEPTH + 1) // 2
N_CONV = DEPTH // 2
EPS = 1e-6

kernel_name = "hybrid_mla_shortconv_ple"

def rmsnorm(x, g):
    x32 = x.astype(jnp.float32)
    y = x32 * lax.rsqrt(jnp.mean(x32 * x32, axis=-1, keepdims=True) + EPS)
    return (y * g.astype(jnp.float32)).astype(x.dtype)

def rope_tables(positions):
    inv_freq = ROPE_THETA ** (-jnp.arange(0, QK_ROPE, 2, dtype=jnp.float32) / QK_ROPE)
    ang = positions.astype(jnp.float32)[..., None] * inv_freq
    return jnp.cos(ang)[:, :, None, :], jnp.sin(ang)[:, :, None, :]

def apply_rope_tail(t, cos, sin):
    t_nope, t_rope = t[..., :QK_NOPE], t[..., QK_NOPE:]
    r1, r2 = jnp.split(t_rope, 2, axis=-1)
    c, s = cos.astype(t.dtype), sin.astype(t.dtype)
    rot = jnp.concatenate([r1 * c - r2 * s, r2 * c + r1 * s], axis=-1)
    return jnp.concatenate([t_nope, rot], axis=-1)

def causal_block_attention(q, k, v):
    bsz, s_len, h, dq = q.shape
    nb = s_len // Q_BLOCK
    qb = q.reshape(bsz, nb, Q_BLOCK, h, dq).transpose(1, 0, 2, 3, 4)
    k_pos = jnp.arange(s_len)
    scale = dq ** -0.5

    def one_block(args):
        q_blk, j = args
        s = jnp.einsum('bqhd,bkhd->bhqk', q_blk, k, preferred_element_type=jnp.float32) * scale
        q_pos = j * Q_BLOCK + jnp.arange(Q_BLOCK)
        mask = k_pos[None, :] <= q_pos[:, None]
        s = jnp.where(mask, s, -jnp.inf)
        pr = jax.nn.softmax(s, axis=-1).astype(v.dtype)
        return jnp.einsum('bhqk,bkhd->bqhd', pr, v)

    o = lax.map(one_block, (qb, jnp.arange(nb)))
    return o.transpose(1, 0, 2, 3, 4).reshape(bsz, s_len, h, v.shape[-1])

def mla_mixer(u, w_in, q_norm_g, kv_norm_g, w_q_up, w_kv_up, qn_g, kn_g, w_out, cos, sin):
    bsz, s_len, _ = u.shape
    z = u @ w_in
    c_q, c_kv, k_rope, gate = jnp.split(
        z, [Q_LORA, Q_LORA + KV_LORA, Q_LORA + KV_LORA + QK_ROPE], axis=-1)
    q = (rmsnorm(c_q, q_norm_g) @ w_q_up).reshape(bsz, s_len, N_HEADS, QK_HEAD)
    kv = (rmsnorm(c_kv, kv_norm_g) @ w_kv_up).reshape(bsz, s_len, N_HEADS, QK_NOPE + V_HEAD)
    k_nope, v = kv[..., :QK_NOPE], kv[..., QK_NOPE:]
    k_rope_h = jnp.broadcast_to(k_rope[:, :, None, :], (bsz, s_len, N_HEADS, QK_ROPE))
    k = jnp.concatenate([k_nope, k_rope_h], axis=-1)
    q = apply_rope_tail(rmsnorm(q, qn_g), cos, sin)
    k = apply_rope_tail(rmsnorm(k, kn_g), cos, sin)
    o = causal_block_attention(q, k, v).reshape(bsz, s_len, ATT_WIDTH)
    return (jax.nn.silu(gate) * o) @ w_out

def shortconv_mixer(u, w_in, conv_w, w_out):
    z = u @ w_in
    b_gate, c_gate, hid, gate = jnp.split(z, 4, axis=-1)
    t = c_gate * hid
    t = lax.conv_general_dilated(
        t, conv_w[:, None, :].astype(t.dtype), window_strides=(1,), padding=[(CONV_K - 1, 0)],
        dimension_numbers=('NWC', 'WIO', 'NWC'), feature_group_count=CONV_WIDTH)
    return (jax.nn.silu(gate) * b_gate * t) @ w_out

def setup_inputs(seed: int = 0) -> dict:
    key = jax.random.key(seed)
    ks = jax.random.split(key, 24)
    nrm = lambda k, shape, fan: jax.random.normal(k, shape, jnp.float32) * (fan ** -0.5)
    gain = lambda k, shape: 1.0 + 0.05 * jax.random.normal(k, shape, jnp.float32)
    x = jax.random.normal(ks[0], (BATCH, SEQ, D_MODEL), jnp.float32)
    p = jax.random.normal(ks[1], (DEPTH, BATCH, SEQ, PLE_DIM), jnp.float32)
    offset = jax.random.randint(ks[2], (BATCH, 1), 0, 1024, dtype=jnp.int32)
    positions = offset + jnp.arange(SEQ, dtype=jnp.int32)[None, :]
    norm_g = gain(ks[3], (DEPTH, D_MODEL))
    a_w_in = nrm(ks[4], (N_MLA, D_MODEL, Q_LORA + KV_LORA + QK_ROPE + ATT_WIDTH), D_MODEL)
    a_q_norm_g = gain(ks[5], (N_MLA, Q_LORA))
    a_kv_norm_g = gain(ks[6], (N_MLA, KV_LORA))
    a_w_q_up = nrm(ks[7], (N_MLA, Q_LORA, N_HEADS * QK_HEAD), Q_LORA)
    a_w_kv_up = nrm(ks[8], (N_MLA, KV_LORA, N_HEADS * (QK_NOPE + V_HEAD)), KV_LORA)
    a_qn_g = gain(ks[9], (N_MLA, QK_HEAD))
    a_kn_g = gain(ks[10], (N_MLA, QK_HEAD))
    a_w_out = nrm(ks[11], (N_MLA, ATT_WIDTH, D_MODEL), ATT_WIDTH)
    b_w_in = nrm(ks[12], (N_CONV, D_MODEL, 4 * CONV_WIDTH), D_MODEL)
    b_conv_w = nrm(ks[13], (N_CONV, CONV_K, CONV_WIDTH), CONV_K)
    b_w_out = nrm(ks[14], (N_CONV, CONV_WIDTH, D_MODEL), CONV_WIDTH)
    ple_w_proj = nrm(ks[15], (DEPTH, PLE_DIM, D_MODEL), PLE_DIM)
    ple_norm_g = gain(ks[16], (DEPTH, D_MODEL))
    ple_w_gate = nrm(ks[17], (DEPTH, D_MODEL, D_MODEL), D_MODEL)
    ple_b_gate = 0.02 * jax.random.normal(ks[18], (DEPTH, D_MODEL), jnp.float32)
    return {"x": x, "p": p, "positions": positions, "norm_g": norm_g,
            "a_w_in": a_w_in, "a_q_norm_g": a_q_norm_g, "a_kv_norm_g": a_kv_norm_g,
            "a_w_q_up": a_w_q_up, "a_w_kv_up": a_w_kv_up, "a_qn_g": a_qn_g, "a_kn_g": a_kn_g,
            "a_w_out": a_w_out, "b_w_in": b_w_in, "b_conv_w": b_conv_w, "b_w_out": b_w_out,
            "ple_w_proj": ple_w_proj, "ple_norm_g": ple_norm_g, "ple_w_gate": ple_w_gate,
            "ple_b_gate": ple_b_gate}

def reference(x, p, positions, norm_g, a_w_in, a_q_norm_g, a_kv_norm_g, a_w_q_up, a_w_kv_up,
              a_qn_g, a_kn_g, a_w_out, b_w_in, b_conv_w, b_w_out, ple_w_proj, ple_norm_g,
              ple_w_gate, ple_b_gate):
    cos, sin = rope_tables(positions)
    h = x
    for i in range(DEPTH):
        u = rmsnorm(h, norm_g[i])
        j = i // N_MIXERS
        if i % N_MIXERS == 0:
            y = mla_mixer(u, a_w_in[j], a_q_norm_g[j], a_kv_norm_g[j], a_w_q_up[j],
                          a_w_kv_up[j], a_qn_g[j], a_kn_g[j], a_w_out[j], cos, sin)
        else:
            y = shortconv_mixer(u, b_w_in[j], b_conv_w[j], b_w_out[j])
        h = h + y
        e = rmsnorm(p[i] @ ple_w_proj[i], ple_norm_g[i])
        h = h + jax.nn.sigmoid(h @ ple_w_gate[i] + ple_b_gate[i]) * e
    return h


_drawn_inputs = setup_inputs


def setup_inputs(seed=0):
    import zlib

    import numpy as np

    out = dict(_drawn_inputs(seed))
    spreads = {}
    factors = {'a_q_norm_g': 8.0,
     'a_kv_norm_g': 8.0,
     'a_qn_g': 8.0,
     'a_kn_g': 8.0,
     'ple_b_gate': 64.0,
     'ple_norm_g': 5.997}
    for name, (base, spread) in spreads.items():
        noise = np.random.default_rng([zlib.crc32(name.encode()), seed]).standard_normal(out[name].shape)
        drawn = base * np.exp(spread * noise) if base else spread * noise
        out[name] = __import__('jax').numpy.asarray(drawn.astype(out[name].dtype))
    for name, factor in factors.items():
        out[name] = (out[name] * factor).astype(out[name].dtype)
    return out
```

```python
from contextlib import ExitStack

import numpy as np
import concourse.bass as bass
import concourse.mybir as mybir

F32 = mybir.dt.float32
F32R = mybir.dt.float32r
I32 = mybir.dt.int32
ALU = mybir.AluOpType
ACT = mybir.ActivationFunctionType
AX = mybir.AxisListType

P = 128
D = 2048
T = 512
KT = D // P
TT = T // P
PLE = 256
PLE_KT = PLE // P
HEADS = 16
PAIRS = HEADS // 2
LORA = 512
LT = LORA // P
NOPE, ROPE, VH = 128, 64, 128
QKH = NOPE + ROPE
HALF = ROPE // 2
TAPS = 3
EPS = 1e-6
THETA = 10000.0
MASKED = -1e30

RING = 8
RAW = 4
SLOT = 512
KPS = SLOT // P
SPT = KT // KPS
STAGES = [
    ("c", 2 * LT * SPT, SLOT), ("kr", RING, KT // RING * ROPE), ("gate", KT * SPT, SLOT),
    ("qkv", PAIRS * RING, SLOT), ("aout", KT * SPT, SLOT), ("e0", RING, SLOT), ("ple0", KT * SPT, SLOT),
    ("conv", 4 * KT * SPT, SLOT), ("bout", KT * SPT, SLOT), ("e1", RING, SLOT), ("ple1", KT * SPT, SLOT),
]
FIRST_SLOT = {}
_n = 0
for _name, _slots, _ in STAGES:
    FIRST_SLOT[_name] = _n
    _n += _slots
SLOTS = _n
QW = 2 * QKH

COLS = {}
_c = 0
for _name, _w in [("norm0", KT), ("norm1", KT), ("kvg", LT), ("qg", LT), ("qn", 1), ("kn", 1), ("pleg0", KT),
                  ("pleg1", KT), ("pleb0", KT), ("pleb1", KT), ("conv", TAPS * KT), ("qrope", ROPE),
                  ("krope", ROPE), ("freq", HALF)]:
    COLS[_name] = _c
    _c += _w
NCOLS = _c

WARM_PRODUCTS = 16
X_CHUNKS = ((0, 2), (2, 4), (4, 8), (8, 12), (12, KT))
X_AFTER = {3: 2, 5: 3, 7: 4}
assert RING == 2 * SPT

S_AT = {3: 0, 2: 512, 0: 896, 1: 1024}
PT_AT = {0: 0, 1: 512, 3: 896, 2: 1024}
J_GROUPS = ((3,), (2, 0), (1,))
J_ORDER = tuple(j for group in J_GROUPS for j in group)
PACKED = P * TT * (TT + 1) // 2
PT_PARTS = ((0, 512), (512, 1024), (1024, PACKED))


def build(nc, A, out):
    ctx = ExitStack()
    with ctx:
        def sb(name, shape, dt=F32, stack=ctx):
            return stack.enter_context(nc.sbuf_tensor(name, shape, dt))

        def sem(name):
            return ctx.enter_context(nc.semaphore(name))

        def overlay(name, *variants):
            made, most = {}, 0
            for variant in variants:
                size = 0
                with ExitStack() as stack:
                    for n, shape, dt in variant:
                        made[n] = sb(n, shape, dt, stack)
                        size += 4 * int(np.prod(shape[1:]))
                most = max(most, size)
            sb(name, [P, most // 4])
            return made

        w_raw = sb("w_raw", [P, RAW, SLOT])
        w_hi = sb("w_hi", [P, RING, SLOT], F32R)
        w_lo = sb("w_lo", [P, RING, SLOT], F32R)
        U = overlay("region_u", [("U_hi", [P, KT, T], F32R), ("U_lo", [P, KT, T], F32R)],
                    [("e0_raw", [P, KT, T], F32)])
        V = overlay("region_v", [("V_hi", [P, KT, T], F32R), ("V_lo", [P, KT, T], F32R)],
                    [("e1_raw", [P, KT, T], F32)],
                    [("c_hi", [P, 2 * LT, T], F32R), ("c_lo", [P, 2 * LT, T], F32R), ("x_raw", [P, KT, T], F32)],
                    [("c_pad", [P, 4 * LT, T], F32), ("c_raw", [P, 2 * LT, T], F32)],
                    [("c_pad2", [P, 4 * LT, T], F32), ("kv_raw", [P, TT, 512], F32),
                     ("kT_hi", [P, 3, T], F32R), ("kT_lo", [P, 3, T], F32R),
                     ("qT_hi", [P, 3, T], F32R), ("qT_lo", [P, 3, T], F32R)])
        S = overlay("region_s",
                    [("q_raw", [P, TT, QW], F32), ("v_hi", [P, TT, 2 * VH], F32R), ("v_lo", [P, TT, 2 * VH], F32R),
                     ("probs", [P, PACKED], F32), ("pT_hi", [P, PACKED], F32R), ("pT_lo", [P, PACKED], F32R),
                     ("swapped", [P, TT, 2, ROPE], F32), ("k_rope", [P, TT, 2, ROPE], F32)],
                    [("tile_a", [P, 2, T], F32), ("tile_b", [P, 2, T], F32), ("tile_c", [P, 2, T], F32),
                     ("tile_d", [P, 2, T], F32), ("squares", [P, 2, T], F32), ("total", [P, 2, T], F32),
                     ("p_hi", [P, PLE_KT, T], F32R), ("p_lo", [P, PLE_KT, T], F32R)],
                    [("s_pad", [P, 12, T], F32), ("conv_in", [P, T + TAPS - 1], F32)])
        gates = sb("gates", [P, 2, T])
        rnorm = sb("rnorm", [P, 3, T])
        cols = sb("cols", [P, NCOLS])
        ident = sb("ident", [P, P])
        ident_r = sb("ident_r", [P, P], F32R)
        mask = sb("mask", [P, P])
        mask_r = sb("mask_r", [P, P], F32R)
        ones = sb("ones", [P, P])
        minus_half = sb("minus_half", [P, 2 * TT])
        eps_col = sb("eps_col", [P, 1])
        pos_i = sb("pos_i", [P, TT], I32)
        pos_f = sb("pos_f", [P, TT])
        tables = sb("tables", [P, 2, 2, TT, ROPE])
        kr_rot = sb("kr_rot", [P, TT, ROPE])
        ss_kr = sb("ss_kr", [P, TT])
        ss_k = sb("ss_k", [P, TT, 2])
        ss_q = sb("ss_q", [P, TT, 2])
        ss_sum = sb("ss_sum", [P, TT, 2])
        var_k = sb("var_k", [P, TT, 2])
        var_q = sb("var_q", [P, TT, 2])
        rstd_k = sb("rstd_k", [P, TT, 2])
        scale_q = sb("scale_q", [P, TT, 2])
        peak = sb("peak", [P, TT])
        shift = sb("shift", [P, TT])
        row_sum = sb("row_sum", [P, TT])
        row_inv = sb("row_inv", [P, TT])
        U_hi, U_lo, V_hi, V_lo = U["U_hi"], U["U_lo"], V["V_hi"], V["V_lo"]
        tile_a, tile_b, tile_c, tile_d = S["tile_a"], S["tile_b"], S["tile_c"], S["tile_d"]
        squares, total = S["squares"], S["total"]
        q_raw, kv_raw = S["q_raw"], V["kv_raw"]
        heads4 = q_raw[:].rearrange("p t (h f) -> p t h f", h=2)
        keys4 = kv_raw[:, :, 0:2 * NOPE].rearrange("p t (h f) -> p t h f", h=2)

        banks = ctx.enter_context(nc.psum_tensor("banks", [P, 8, 512], F32))
        flat_banks = banks[:].rearrange("p b n -> p (b n)")

        def scores_of(late):
            at = SLOT if late else 4 * SLOT
            return flat_banks[:, at:at + 3 * SLOT]

        def probs_of(late):
            return S["q_raw"][:].rearrange("p t f -> p (t f)") if late else S["probs"][:]

        STAT_BANK, KR_BANK, KR_TURN_BANK, O_BANK = 4, 6, 7, 7
        TURNS = (("k", 0), ("k", 2), ("q", 0), ("q", 2), ("k", 1), ("q", 1))
        TURN_BANK = (0, 1, 2, 3, 0, 1)
        TURN_GAIN = ("kn", None, "qn", None, "kn", "qn")

        gate_dram = nc.dram_tensor("gate_spill", [KT, P, T], F32, kind="Internal").ap()
        h2_dram = nc.dram_tensor("h2_spill", [KT, P, T], F32, kind="Internal").ap()

        raw_loaded = [sem(f"raw_loaded{i}") for i in range(RAW)]
        weights_hi = sem("weights_hi")
        weights_split = sem("weights_split")
        weights_used = sem("weights_used")
        cols_loaded, x_loaded = sem("cols_loaded"), [sem(f"x_loaded{i}") for i in range(len(X_CHUNKS))]
        pos_loaded = sem("pos_loaded")
        consts_ready, consts_r = sem("consts_ready"), sem("consts_rounded")
        u_hi, u_split = sem("u0_hi"), sem("u0_split")
        squared, summed = sem("squared"), sem("squares_summed")
        stat_done, root_done, rnorm_done = sem("stat_done"), sem("root_done"), sem("rnorm_done")
        rnorm_sq = sem("rnorm_squared")

        class Stage:

            def __init__(self, name, tiles, before):
                self.name, self.tiles, self.before = name, tiles, before
                self.taken = sem(f"{name}_taken")
                self.slot = FIRST_SLOT[name]

        st_c = Stage("c", 2 * LT, None)
        st_gate = Stage("gate", KT, st_c)
        st_aout = Stage("aout", KT, None)
        st_ple0 = Stage("ple0", KT, st_aout)
        st_conv = Stage("conv", 4 * KT, st_ple0)
        st_bout = Stage("bout", KT, st_conv)
        st_ple1 = Stage("ple1", KT, st_bout)

        kr_scaled, kr_turned, kr_ready = sem("kr_scaled"), sem("kr_turned"), sem("kr_ready")
        c_normed, c_hi_done, c_split = sem("c_normed"), sem("c_hi_done"), sem("c_split")
        table_step, angles_ready, sines_ready, tables_ready = (
            sem("table_step"), sem("angles_ready"), sem("sines_ready"), sem("tables_ready"))
        gate_ready, gate_saved = sem("gate_ready"), [sem(f"gate_saved{i}") for i in range(2)]

        proj_done, proj_copied, proj_raw = sem("proj_done"), sem("proj_copied"), sem("proj_raw")
        ss_added, var_k_ready, rstd_k_ready = sem("ss_added"), sem("var_k_ready"), sem("rstd_k_ready")
        var_q_ready, scale_q_ready = sem("var_q_ready"), sem("scale_q_ready")
        k_scaled, rope_terms, q_roped = sem("k_scaled"), sem("rope_terms"), sem("q_roped")
        heads_turned, heads_hi, heads_split = sem("heads_turned"), sem("heads_hi"), sem("heads_split")
        v_hi_done, v_split = sem("v_hi_done"), sem("v_split")
        scores_done, peak_ready, shift_ready = sem("scores_done"), sem("peak_ready"), sem("shift_ready")
        exp_done, inv_ready, probs_ready = sem("exp_done"), sem("inv_ready"), sem("probs_ready")
        probs_turned, pT_hi_done, pT_split = sem("probs_turned"), sem("pT_hi_done"), sem("pT_split")
        pv_done, y_ready, y_hi_done, y_split = sem("pv_done"), sem("y_ready"), sem("y_hi_done"), sem("y_split")
        gate_loaded = [sem(f"gate_loaded{i}") for i in range(2)]

        class Out:

            def __init__(self, name):
                self.res_loaded = [sem(f"{name}_res_loaded{i}") for i in range(2)]
                self.h_hi, self.h_split = sem(f"{name}_h_hi"), sem(f"{name}_h_split")

        class Ple:

            def __init__(self, name):
                self.p_loaded, self.p_hi, self.p_split = sem(f"{name}_p_loaded"), sem(f"{name}_p_hi"), sem(f"{name}_p_split")
                self.e_done = sem(f"{name}_e_done")
                self.e_normed, self.h_joined, self.gated = (
                    sem(f"{name}_e_normed"), sem(f"{name}_h_joined"), sem(f"{name}_gated"))
                self.h_ready, self.u_hi, self.u_split = sem(f"{name}_h_ready"), sem(f"{name}_u_hi"), sem(f"{name}_u_split")
                self.stored = [sem(f"{name}_stored{i}") for i in range(2)]

        out_a, out_b = Out("aout"), Out("bout")
        ple_a, ple_b = Ple("ple0"), Ple("ple1")
        conv_part, tap_done = sem("conv_part"), sem("tap_done")
        silu_done, conv_ready = sem("silu_done"), sem("conv_ready")
        yc_hi, yc_split = sem("yc_hi"), sem("yc_split")
        pad_zero = sem("pad_zero")

        SQ_X, SQ_C, SQ_E0 = 0, KT, KT + 2 * LT
        SQ_H2, SQ_E1 = SQ_E0 + KT, SQ_E0 + 2 * KT
        STAT_X, STAT_KV, STAT_Q, STAT_E0, STAT_H2, STAT_E1 = range(6)
        STAT_AT = {STAT_X: 0, STAT_KV: 1, STAT_Q: 2, STAT_E0: 1, STAT_H2: 0, STAT_E1: 1}
        STAT_OF = {STAT_X: D, STAT_KV: LORA, STAT_Q: LORA, STAT_E0: D, STAT_H2: D, STAT_E1: D}
        R_SQUARE = 2

        def col(name, n=0, width=1):
            at = COLS[name]
            if isinstance(n, int):
                return cols[:, at + n:at + n + width]
            return cols[:, bass.ds(n + at, width)]

        def f32(ap):
            return ap.bitcast(F32)

        def loop(eng, n, body):
            body(0, True, n == 1)
            if n > 3:
                with eng.Fori(1, n - 1) as i:
                    body(i, False, False)
            elif n == 3:
                body(1, False, False)
            if n > 1:
                body(n - 1, False, True)

        KR_SLOTS = range(FIRST_SLOT["kr"], FIRST_SLOT["kr"] + RING)

        def kr_slot(s0):
            raw = w_raw[:, s0 % RAW, 0:KT // RING * ROPE].rearrange("p (b f) -> p b f", f=ROPE)
            both = w_hi[:, s0 % RING, 0:KT // RING * 2 * ROPE].rearrange("p (b s f) -> p b s f", s=2, f=ROPE)
            return raw, both[:, :, 0, :], both[:, :, 1, :]

        def slot_hi(s0, adv=0):
            if isinstance(adv, int) and s0 + adv >= SLOTS:
                return
            act = nc.scalar
            act.wait_ge(raw_loaded[s0 % RAW], adv * (16 // RAW) + 16 * (s0 // RAW + 1))
            if not isinstance(adv, int) or s0 + adv >= RING:
                act.wait_ge(weights_used, adv + (s0 - RING + 1))
            if s0 in KR_SLOTS:
                raw, hi, _ = kr_slot(s0)
                act.activation(hi, raw, ACT.Copy).then_inc(weights_hi, 1)
            else:
                act.activation(w_hi[:, s0 % RING, :], w_raw[:, s0 % RAW, :], ACT.Copy).then_inc(weights_hi, 1)

        def slot_lo(s0, adv=0):
            if isinstance(adv, int) and s0 + adv >= SLOTS:
                return
            dve = nc.vector
            dve.wait_ge(weights_hi, adv + (s0 + 1))
            if s0 in KR_SLOTS:
                raw, hi, lo = kr_slot(s0)
                dve.tensor_tensor(lo, raw, f32(hi), ALU.subtract).then_inc(weights_split, 1)
            else:
                dve.tensor_tensor(w_lo[:, s0 % RING, :], w_raw[:, s0 % RAW, :], f32(w_hi[:, s0 % RING, :]),
                                  ALU.subtract).then_inc(weights_split, 1)

        def tile_done(eng, st, i, t):
            eng.wait_ge(weights_used, i * 4 * SPT + (st.slot + SPT * (t + 1)))

        def split_slots(step, s0, adv, n):
            for k in range(n):
                step(s0 + k, adv)

        def load_x(eng, c):
            a, b = X_CHUNKS[c]
            eng.dma_start(V["x_raw"][:, a:b, :], A["x"][a:b].rearrange("k p n -> p k n")).then_inc(x_loaded[c], 16)

        block = ctx.enter_context(nc.Block())

        @block.sync
        def _(sp):
            for name, slots, width in STAGES:
                src, s0 = A["w_" + name], FIRST_SLOT[name]

                def turn(i, first):
                    for k in range(RING):
                        if not (first and s0 + k < RAW):
                            sp.wait_ge(weights_split, i * RING + (s0 + k - RAW + 1))
                        if name == "qkv" and k >= RING // 2:
                            w = QW
                        else:
                            w = width
                        sp.dma_start(w_raw[:, k % RAW, 0:w], src[i * RING + k, :, 0:w]).then_inc(
                            raw_loaded[k % RAW], 16)
                        if first and s0 + k in X_AFTER:
                            load_x(sp, X_AFTER[s0 + k])
                        if first and s0 + k == RING - 1:
                            sp.dma_start(pos_i[:], A["pos"]).then_inc(pos_loaded, 16)

                turn(0, True)
                if slots > RING:
                    with sp.Fori(1, slots // RING) as i:
                        turn(i, False)

        @block.gpsimd
        def _(pool):
            pool.memset(ident[:], 0.0).then_inc(consts_ready, 1)
            pool.memset(mask[:], 0.0).then_inc(consts_ready, 1)
            pool.memset(ones[:], 1.0).then_inc(consts_ready, 1)
            pool.memset(minus_half[:], -0.5).then_inc(consts_ready, 1)
            pool.memset(eps_col[:], EPS).then_inc(consts_ready, 1)
            pool.wait_ge(consts_ready, 5)
            pool.affine_select(out=ident[:], in_=ident[:], compare_op=ALU.not_equal, fill=1.0, base=0,
                               pattern=[[-1, P]], channel_multiplier=1).then_inc(consts_ready, 1)
            pool.affine_select(out=mask[:], in_=mask[:], compare_op=ALU.is_ge, fill=MASKED, base=0,
                               pattern=[[-1, P]], channel_multiplier=1).then_inc(consts_ready, 1)

            flat = "p t h -> p (t h)"

            def key_root(p):
                pool.wait_ge(var_k_ready, p + 1)
                pool.tensor_tensor(rstd_k[:].rearrange(flat), var_k[:].rearrange(flat), minus_half[:],
                                   ALU.pow).then_inc(rstd_k_ready, 1)

            def query_root(p):
                pool.wait_ge(var_q_ready, p + 1)
                pool.tensor_tensor(scale_q[:].rearrange(flat), var_q[:].rearrange(flat), minus_half[:],
                                   ALU.pow).then_inc(scale_q_ready, 1)

            def v_rest(p):
                pool.wait_ge(v_hi_done, p + 1)
                pool.tensor_tensor(S["v_lo"][:], kv_raw[:, :, 2 * NOPE:], f32(S["v_hi"][:]), ALU.subtract).then_inc(
                    v_split, 1)

            def y_rest(p, h):
                pool.wait_ge(y_hi_done, p * 2 + (h + 1))
                pool.tensor_tensor(U_lo[:, p * 2 + h, :], gates[:, h, :], f32(U_hi[:, p * 2 + h, :]),
                                   ALU.subtract).then_inc(y_split, 1)

            def attend(p, first, last):
                if not last:
                    key_root(p + 1)
                y_rest(p, 0)
                if not last:
                    query_root(p + 1)
                    v_rest(p + 1)
                y_rest(p, 1)

            key_root(0)
            query_root(0)
            v_rest(0)
            loop(pool, PAIRS, attend)

        @block.tensor
        def _(pe):
            def split_mm(dst, parts, start, stop):
                sh, sl, mh, ml = parts
                pe.matmul(dst, sh, mh, start=start, stop=False)
                pe.matmul(dst, sh, ml, start=False, stop=False)
                return pe.matmul(dst, sl, mh, start=False, stop=stop)

            def dense_tile(st, n, adv, t, mov_hi, mov_lo, moving_ready=None, quarters=range(SPT)):
                if isinstance(n, int) and n < 4:
                    if st.before is not None:
                        pe.wait_ge(st.before.taken, st.before.tiles - 4 + n + 1)
                else:
                    pe.wait_ge(st.taken, n - 3)
                for q in quarters:
                    s0 = st.slot + SPT * t + q
                    pe.wait_ge(weights_split, adv + (s0 + 1))
                    for b in range(KPS):
                        k = q * KPS + b
                        if moving_ready is not None:
                            moving_ready(k)
                        w = slice(b * P, (b + 1) * P)
                        mm = split_mm(banks[:, t, :], (w_hi[:, s0 % RING, w], w_lo[:, s0 % RING, w],
                                                       mov_hi[:, k, :], mov_lo[:, k, :]), k == 0, k == KT - 1)
                    mm.then_inc(weights_used, 1)

            def dense(st, mov_hi, mov_lo, ready_sem, hooks=None, done=0):
                def turn(i, first, last):
                    for t in range(done if first else 0, 4):
                        ready = (lambda k: pe.wait_ge(ready_sem, k + 1)) if first and t == 0 and ready_sem else None
                        dense_tile(st, i * 4 + t, i * 16, t, mov_hi, mov_lo, ready)
                        if first and hooks and t in hooks:
                            hooks[t]()
                loop(pe, st.tiles // 4, turn)

            def sum_features(stat, sq_to, row, bank):
                pe.wait_ge(summed, sq_to)
                if stat:
                    pe.wait_ge(root_done, stat if bank == STAT_BANK else stat - 1)
                pe.matmul(banks[:, bank, :], ones[:], total[:, row, :], start=True, stop=True).then_inc(stat_done, 1)

            pe.wait_ge(consts_ready, 7)
            for _ in range(WARM_PRODUCTS):
                pe.matmul(banks[:, KR_BANK, 0:P], ones[:], ones[:], start=True, stop=True)

            for q in range(SPT):
                for b in range(KPS):
                    k = q * KPS + b
                    pe.wait_ge(u_split, k + 1)
                    for t in range(2):
                        s0 = 2 * q + t
                        if b == 0:
                            pe.wait_ge(weights_split, s0 + 1)
                        w = slice(b * P, (b + 1) * P)
                        mm = split_mm(banks[:, t, :], (w_hi[:, s0, w], w_lo[:, s0, w], U_hi[:, k, :], U_lo[:, k, :]),
                                      k == 0, k == KT - 1)
                        if b == KPS - 1:
                            mm.then_inc(weights_used, 1)
            for n in range(2, 2 * LT):
                dense_tile(st_c, n, n // 4 * 16, n % 4, U_hi, U_lo)
                if n == 2:
                    sum_features(STAT_X, SQ_X + KT, 0, STAT_BANK)
            for q in range(RING):
                s0 = FIRST_SLOT["kr"] + q
                pe.wait_ge(weights_split, s0 + 1)
                for b in range(KT // RING):
                    k = q * (KT // RING) + b
                    w = slice(b * 2 * ROPE, (b + 1) * 2 * ROPE)
                    pe.matmul(banks[:, KR_BANK, :], w_hi[:, s0 % RING, w], U_hi[:, k, :], start=k == 0, stop=False)
                    mm = pe.matmul(banks[:, KR_BANK, :], w_hi[:, s0 % RING, w], U_lo[:, k, :], start=False,
                                   stop=k == KT - 1)
                mm.then_inc(weights_used, 1)

            def turn_kr():
                pe.wait_ge(kr_scaled, 1)
                for t in range(TT):
                    mm = pe.transpose(banks[:, KR_TURN_BANK, t * P:(t + 1) * P], tile_a[:, 0, t * P:(t + 1) * P],
                                      ident[:])
                mm.then_inc(kr_turned, 1)
                sum_features(STAT_KV, SQ_C + LT, 0, STAT_BANK)
                sum_features(STAT_Q, SQ_C + 2 * LT, 1, STAT_BANK + 1)

            dense(st_gate, U_hi, U_lo, None, {0: turn_kr})

            c_hi, c_lo = V["c_hi"], V["c_lo"]
            kT_hi, kT_lo, qT_hi, qT_lo = V["kT_hi"], V["kT_lo"], V["qT_hi"], V["qT_lo"]
            v_hi, v_lo, pT_hi, pT_lo = S["v_hi"], S["v_lo"], S["pT_hi"], S["pT_lo"]

            def project(p, t, part):
                if part == 1:
                    pe.wait_ge(proj_raw, p * 8 + (t + 1))
                elif t < 2 and not (isinstance(p, int) and p == 0):
                    pe.wait_ge(heads_split, p * 6 + (t - 1))
                width, c0 = (512, 0) if part == 0 else (QW, LT)
                for k in range(LT):
                    s0 = FIRST_SLOT["qkv"] + 4 * part + k
                    if t == 0:
                        pe.wait_ge(weights_split, p * RING + (s0 + 1))
                    tok = slice(t * P, (t + 1) * P)
                    mm = split_mm(banks[:, t, 0:width],
                                  (c_hi[:, c0 + k, tok], c_lo[:, c0 + k, tok],
                                   w_hi[:, s0 % RING, 0:width], w_lo[:, s0 % RING, 0:width]), k == 0, k == LT - 1)
                    if t == TT - 1:
                        mm.then_inc(weights_used, 1)
                if t < TT - 1:
                    mm.then_inc(proj_done, 1)

            def turn_heads(p, x):
                of, row = TURNS[x]
                if x < TT:
                    pe.wait_ge(proj_raw, p * 8 + (TT + x + 1))
                else:
                    pe.wait_ge(heads_split, p * 6 + (x - TT + 1))
                if x == 0:
                    pe.wait_ge(k_scaled, p + 1)
                if x == 2:
                    pe.wait_ge(proj_copied, p * 8 + 8)
                if x == 3:
                    pe.wait_ge(q_roped, p * 2 + 2)
                for t in range(TT):
                    if row == 2:
                        src = S["k_rope" if of == "k" else "swapped"][:, t, :, :].rearrange("p h f -> p (h f)")
                    else:
                        src = keys4[:, t, row, :] if of == "k" else heads4[:, t, row, 0:NOPE]
                    mm = pe.transpose(banks[:, TURN_BANK[x], t * P:(t + 1) * P], src, ident[:])
                mm.then_inc(heads_turned, 1)

            def score(p, first, h, late=False):
                scores = scores_of(late)
                pe.wait_ge(heads_split, p * 6 + (6 if h else 3))
                if not (first and h == 0) and not late:
                    pe.wait_ge(pT_split, p * 6 + 3 * h)
                for j in J_ORDER:
                    n = (j + 1) * P
                    dst = scores[:, S_AT[j]:S_AT[j] + n]
                    q, r = slice(j * P, (j + 1) * P), slice(h * ROPE, (h + 1) * ROPE)
                    pe.matmul(dst, qT_hi[:, h, q], kT_hi[:, h, 0:n], start=True, stop=False)
                    pe.matmul(dst[:, j * P:n], ident_r[:], mask_r[:], start=False, stop=False)
                    pe.matmul(dst, qT_hi[:, h, q], kT_lo[:, h, 0:n], start=False, stop=False)
                    pe.matmul(dst, qT_lo[:, h, q], kT_hi[:, h, 0:n], start=False, stop=False)
                    if h == 0 and j == J_ORDER[0]:
                        pe.wait_ge(heads_split, p * 6 + 4)
                    mm = split_mm(dst, (qT_hi[r, 2, q], qT_lo[r, 2, q], kT_hi[r, 2, 0:n], kT_lo[r, 2, 0:n]),
                                  False, True)
                    if j != 2:
                        mm.then_inc(scores_done, 1)

            def turn_probs(p, h, late=False):
                scores, probs = scores_of(late), probs_of(late)
                pe.wait_ge(probs_ready, p * 8 + 4 * (h + 1))
                for group in ((0,), (1, 3), (2,)):
                    for k in group:
                        for j in range(k, TT):
                            at = PT_AT[k] + (j - k) * P
                            mm = pe.transpose(scores[:, at:at + P], probs[:, S_AT[j] + k * P:S_AT[j] + (k + 1) * P],
                                              ident[:])
                    mm.then_inc(probs_turned, 1)

            def weigh_values(p, first, h, parts=((1, 0), (2, 1), (2, 3), (3, 2))):
                if h == 0:
                    pe.wait_ge(v_split, p + 1)
                if not (first and h == 0) and parts[0][1] == 0:
                    pe.wait_ge(y_ready, p * 2 + h)
                for part, k in parts:
                    pe.wait_ge(pT_split, p * 6 + (3 * h + part))
                    src = slice(PT_AT[k], PT_AT[k] + (TT - k) * P)
                    mm = split_mm(banks[:, O_BANK, k * P:], (v_hi[:, k, h * VH:(h + 1) * VH], v_lo[:, k, h * VH:(h + 1) * VH],
                                                             pT_hi[:, src], pT_lo[:, src]), k == 0, k == 2)
                    if k == 2:
                        mm.then_inc(pv_done, 1)

            def begin_aout(q):
                dense_tile(st_aout, 0, 0, 0, U_hi, U_lo, lambda k: pe.wait_ge(y_split, k + 1), (q,))

            def attend(p, first, last):
                score(p, first, 0)
                if not last:
                    for t in range(3):
                        project(p + 1, t, 0)
                if last:
                    score(p, first, 1, True)
                turn_probs(p, 0)
                if last:
                    begin_aout(0)
                else:
                    project(p + 1, 3, 0)
                weigh_values(p, first, 0)
                if not last:
                    score(p, first, 1)
                    for t in range(3):
                        project(p + 1, t, 1)
                else:
                    begin_aout(1)
                turn_probs(p, 1, last)
                if last:
                    begin_aout(2)
                else:
                    turn_heads(p + 1, 0)
                    project(p + 1, 3, 1)
                    turn_heads(p + 1, 1)
                weigh_values(p, first, 1, ((1, 0),))
                if not last:
                    for x in range(2, 5):
                        turn_heads(p + 1, x)
                weigh_values(p, first, 1, ((2, 1), (2, 3), (3, 2)))
                if not last:
                    turn_heads(p + 1, 5)

            pe.wait_ge(consts_r, 2)
            pe.wait_ge(c_split, 2 * LT)
            for t in range(TT):
                pe.wait_ge(st_gate.taken, KT - TT + t + 1)
                project(0, t, 0)
            for t in range(3):
                project(0, t, 1)
            turn_heads(0, 0)
            project(0, 3, 1)
            for x in range(1, 6):
                turn_heads(0, x)
            loop(pe, PAIRS, attend)

            begin_aout(SPT - 1)
            dense(st_aout, U_hi, U_lo, None, done=1)

            def embed(ple, stage, sq0):
                pe.wait_ge(ple.p_split, PLE_KT)
                for n in range(KT):
                    s0 = FIRST_SLOT[stage] + n // 2
                    if n % 2 == 0:
                        pe.wait_ge(weights_split, s0 + 1)
                    if n >= 4:
                        pe.wait_ge(squared, sq0 + n - 3)
                    for k in range(PLE_KT):
                        at = (n % 2) * PLE_KT * P + k * P
                        mm = split_mm(banks[:, 4 + n % 4, :], (w_hi[:, s0 % RING, at:at + P], w_lo[:, s0 % RING, at:at + P],
                                                               S["p_hi"][:, k, :], S["p_lo"][:, k, :]),
                                      k == 0, k == PLE_KT - 1)
                    mm.then_inc(weights_used if n % 2 else ple.e_done, 1)

            pe.wait_ge(y_ready, HEADS)
            embed(ple_a, "e0", SQ_E0)
            dense(st_ple0, V_hi, V_lo, out_a.h_split, {0: lambda: sum_features(STAT_E0, SQ_E0 + KT, 0, STAT_BANK)})

            dense(st_conv, U_hi, U_lo, ple_a.u_split,
                  {0: lambda: sum_features(STAT_H2, SQ_H2 + KT, 1, STAT_BANK)})
            dense(st_bout, V_hi, V_lo, yc_split)
            embed(ple_b, "e1", SQ_E1)
            dense(st_ple1, U_hi, U_lo, out_b.h_split, {0: lambda: sum_features(STAT_E1, SQ_E1 + KT, 0, STAT_BANK)})

        @block.scalar
        def _(act):
            def root(stat, bank):
                act.wait_ge(stat_done, stat + 1)
                act.activation(rnorm[:, STAT_AT[stat], :], banks[:, bank, :], ACT.Sqrt,
                               bias=eps_col[:, 0:1], scale=1.0 / STAT_OF[stat]).then_inc(root_done, 1)

            load_x(act, 0)
            act.dma_start(cols[:], A["cols"]).then_inc(cols_loaded, 16)
            load_x(act, 1)
            x_raw = V["x_raw"]
            for k in range(KT):
                if k % KPS == 0:
                    split_slots(slot_hi, k // 2, 0, 2)
                for c, (a, b) in enumerate(X_CHUNKS):
                    if k == a:
                        act.wait_ge(x_loaded[c], 16)
                if k == 0:
                    act.wait_ge(cols_loaded, 16)
                act.activation(U_hi[:, k, :], x_raw[:, k, :], ACT.Copy, scale=col("norm0", k)).then_inc(u_hi, 1)
            for k in range(KT):
                if k >= 2:
                    act.wait_ge(summed, k - 1)
                act.activation(squares[:, k % 2, :], x_raw[:, k, :], ACT.Square).then_inc(squared, 1)
                if k % KPS == KPS - 1:
                    split_slots(slot_hi, RING + k // 2 - 1, 0, 2)
            act.wait_ge(consts_ready, 7)
            act.activation(ident_r[:], ident[:], ACT.Copy).then_inc(consts_r, 1)
            act.activation(mask_r[:], mask[:], ACT.Copy).then_inc(consts_r, 1)
            c_raw = V["c_raw"]
            for n in range(2 * LT):
                if n > 1:
                    split_slots(slot_hi, st_c.slot + RING + SPT * n, 0, SPT)
                if n == 0:
                    root(STAT_X, STAT_BANK)
                if n == LT:
                    for s in range(2):
                        act.wait_ge(angles_ready, s + 1)
                        act.activation(tile_d[:, s, 0:TT * HALF], tile_c[:, s, 0:TT * HALF], ACT.Sin).then_inc(
                            sines_ready, 1)
                act.wait_ge(st_c.taken, n + 1)
                act.wait_ge(summed, SQ_C + n - 1)
                act.activation(squares[:, n % 2, :], c_raw[:, n, :], ACT.Square).then_inc(squared, 1)
            split_slots(slot_hi, FIRST_SLOT["kr"] + RING, 0, RING)

            def hook(t):
                if t == 0:
                    root(STAT_KV, STAT_BANK)
                    root(STAT_Q, STAT_BANK + 1)
                else:
                    for n in range(3 * t - 3, min(3 * t, 2 * LT)):
                        act.wait_ge(c_normed, n + 1)
                        act.activation(V["c_hi"][:, n, :], tile_b[:, n % 2, :], ACT.Copy).then_inc(c_hi_done, 1)

            def gate_turn(i, first, last):
                for t in range(4):
                    split_slots(slot_hi, st_gate.slot + RING + SPT * t, i * 16, SPT)
                    act.wait_ge(st_gate.taken, i * 4 + (t + 1))
                    act.activation(gates[:, t % 2, :], gates[:, t % 2, :], ACT.Silu).then_inc(gate_ready, 1)
                    act.wait_ge(gate_ready, i * 4 + (t + 1))
                    act.dma_start(gate_dram[i * 4 + t], gates[:, t % 2, :]).then_inc(gate_saved[t % 2], 16)
                    if first:
                        hook(t)

            loop(act, KT // 4, gate_turn)

            kT_hi, qT_hi = V["kT_hi"], V["qT_hi"]
            v_hi, pT_hi = S["v_hi"], S["pT_hi"]

            def load_gate(head, side):
                act.dma_start(gates[:, side, :], gate_dram[head]).then_inc(gate_loaded[side], 16)

            def take(p, first, t, part):
                bank = banks[:, t, :]
                if t < TT - 1:
                    act.wait_ge(proj_done, p * 2 * (TT - 1) + ((TT - 1) * part + t + 1))
                else:
                    act.wait_ge(weights_used, p * RING + (FIRST_SLOT["qkv"] + 4 * (part + 1)))
                if part == 0:
                    if t == 0 and not first:
                        act.wait_ge(v_split, p)
                    act.activation(kv_raw[:, t, :], bank, ACT.Copy).then_inc(proj_copied, 1)
                    act.wait_ge(proj_copied, p * 8 + (t + 1))
                    for h in range(2):
                        mm = act.activation(bank[:, h * NOPE:(h + 1) * NOPE], bank[:, h * NOPE:(h + 1) * NOPE],
                                            ACT.Square, accum_out=ss_k[:, t, h:h + 1])
                else:
                    act.activation(q_raw[:, t, :], bank[:, 0:QW], ACT.Copy).then_inc(proj_copied, 1)
                    act.wait_ge(proj_copied, p * 8 + (TT + t + 1))
                    for h in range(2):
                        mm = act.activation(bank[:, h * QKH:(h + 1) * QKH], bank[:, h * QKH:(h + 1) * QKH],
                                            ACT.Square, accum_out=ss_q[:, t, h:h + 1])
                mm.then_inc(proj_raw, 1)

            def heads_round(p, x):
                (of, row), gain = TURNS[x], TURN_GAIN[x]
                dst = kT_hi if of == "k" else qT_hi
                act.wait_ge(heads_turned, p * 6 + (x + 1))
                act.activation(dst[:, row, :], banks[:, TURN_BANK[x], :], ACT.Copy,
                               scale=col(gain) if gain else 1.0).then_inc(heads_hi, 1)

            def v_round(p):
                act.wait_ge(proj_raw, p * 8 + 4)
                act.activation(v_hi[:], kv_raw[:, :, 2 * NOPE:], ACT.Copy).then_inc(v_hi_done, 1)

            def exponent(p, h, late=False):
                scores, probs = scores_of(late), probs_of(late)
                for n, j in enumerate(J_ORDER):
                    s = slice(S_AT[j], S_AT[j] + (j + 1) * P)
                    act.wait_ge(shift_ready, p * 8 + (4 * h + n + 1))
                    act.activation(probs[:, s], scores[:, s], ACT.Exp, bias=shift[:, j:j + 1],
                                   scale=scale_q[:, j, h:h + 1], accum_out=row_sum[:, j:j + 1]).then_inc(exp_done, 1)

            def probs_round(p, h, parts=(0, 1, 2), late=False):
                scores = scores_of(late)
                for n in parts:
                    a, b = PT_PARTS[n]
                    act.wait_ge(probs_turned, p * 6 + (3 * h + n + 1))
                    act.activation(pT_hi[:, a:b], scores[:, a:b], ACT.Copy).then_inc(pT_hi_done, 1)

            def y_round(p, h):
                act.wait_ge(y_ready, p * 2 + (h + 1))
                act.activation(U_hi[:, p * 2 + h, :], gates[:, h, :], ACT.Copy).then_inc(y_hi_done, 1)

            def attend(p, first, last):
                nxt = FIRST_SLOT["qkv"] + RING + 4
                exponent(p, 0)
                if not first:
                    act.wait_ge(y_split, p * 2)
                    load_gate(p * 2 + 1, 1)
                if not last:
                    for t in range(3):
                        take(p + 1, False, t, 0)
                probs_round(p, 0)
                if last:
                    exponent(p, 1, True)
                else:
                    split_slots(slot_hi, nxt, p * RING, 2)
                    take(p + 1, False, 3, 0)
                    split_slots(slot_hi, nxt + 2, p * RING, 2)
                y_round(p, 0)
                if not last:
                    split_slots(slot_hi, nxt + 4, p * RING, 4)
                if not last:
                    exponent(p, 1)
                    act.wait_ge(y_split, p * 2 + 1)
                    load_gate(p * 2 + 2, 0)
                    for t in range(3):
                        take(p + 1, False, t, 1)
                    heads_round(p + 1, 0)
                probs_round(p, 1, (0, 1), last)
                if not last:
                    take(p + 1, False, 3, 1)
                probs_round(p, 1, (2,), last)
                if last:
                    split_slots(slot_hi, nxt, p * RING, 4)
                else:
                    for x in range(1, 6):
                        heads_round(p + 1, x)
                    act.wait_ge(pv_done, p * 2 + 2)
                    v_round(p + 1)
                y_round(p, 1)

            for side in range(2):
                act.wait_ge(gate_saved[side], 16 * KT // 2)
            for side in range(2):
                load_gate(side, side)
            for t in range(TT):
                take(0, True, t, 0)
            act.wait_ge(kr_ready, 1)
            for t in range(3):
                take(0, True, t, 1)
            heads_round(0, 0)
            take(0, True, 3, 1)
            for x in range(1, 6):
                heads_round(0, x)
            split_slots(slot_hi, FIRST_SLOT["qkv"] + RING, 0, 4)
            v_round(0)
            loop(act, PAIRS, attend)

            def load_res(o, src, n, half):
                act.dma_start(tile_a[:, half, :], src[n]).then_inc(o.res_loaded[half], 16)

            def output(st, o, ple, layer, src, dst_hi):
                load_res(o, src, 0, 0)
                load_res(o, src, 1, 1)
                act.dma_start(gates[:], A["p"][layer].rearrange("k p n -> p k n")).then_inc(ple.p_loaded, 16)

                def turn(i, first, last):
                    for t in range(4):
                        if last and t == 0:
                            act.wait_ge(ple.p_loaded, 16)
                        if last and t < PLE_KT:
                            act.activation(S["p_hi"][:, t, :], gates[:, t, :], ACT.Copy).then_inc(ple.p_hi, 1)
                        split_slots(slot_hi, st.slot + RING + SPT * t, i * 16, SPT)
                        act.wait_ge(st.taken, i * 4 + (t + 1))
                        act.activation(dst_hi[:, i * 4 + t, :], tile_b[:, t % 2, :], ACT.Copy).then_inc(o.h_hi, 1)
                        if not (last and t >= 2):
                            load_res(o, src, i * 4 + (t + 2), t % 2)
                loop(act, KT // 4, turn)

            def embed(ple, stage, e_raw, sq0):
                for n in range(KT):
                    if n % 2:
                        act.wait_ge(weights_used, FIRST_SLOT[stage] + n // 2 + 1)
                    else:
                        act.wait_ge(ple.e_done, n // 2 + 1)
                    act.wait_ge(summed, sq0 + n - 1)
                    act.activation(e_raw[:, n, :], banks[:, 4 + n % 4, :], ACT.Copy)
                    act.activation(squares[:, n % 2, :], banks[:, 4 + n % 4, :], ACT.Square).then_inc(squared, 1)
                    if n % 2:
                        slot_hi(FIRST_SLOT[stage] + RING + n // 2)

            def gated(st, ple, stat, layer, dst_dram, sq0):
                root_at = stat

                def turn(i, first, last):
                    for t in range(4):
                        split_slots(slot_hi, st.slot + RING + SPT * t, i * 16, SPT)
                        if first and t == 0:
                            root(root_at, STAT_BANK)
                        tile_done(act, st, i, t)
                        if not (first and t < 2):
                            act.wait_ge(ple.h_ready, i * 4 + (t - 1))
                        act.activation(tile_a[:, t % 2, :], banks[:, t, :], ACT.Sigmoid,
                                       bias=col(f"pleb{layer}", i * 4 + t)).then_inc(st.taken, 1)
                        act.wait_ge(ple.h_ready, i * 4 + (t + 1))
                        act.dma_start(dst_dram[i * 4 + t], tile_d[:, t % 2, :]).then_inc(ple.stored[t % 2], 16)
                        if layer == 0:
                            act.activation(U_hi[:, i * 4 + t, :], tile_d[:, t % 2, :], ACT.Copy,
                                           scale=col("norm1", i * 4 + t)).then_inc(ple.u_hi, 1)
                            act.wait_ge(summed, i * 4 + (sq0 + t - 1))
                            act.activation(squares[:, t % 2, :], tile_d[:, t % 2, :], ACT.Square).then_inc(squared, 1)
                loop(act, KT // 4, turn)

            act.wait_ge(y_split, HEADS)
            output(st_aout, out_a, ple_a, 0, A["x"], V_hi)
            embed(ple_a, "e0", U["e0_raw"], SQ_E0)
            gated(st_ple0, ple_a, STAT_E0, 0, h2_dram, SQ_H2)

            def conv_turn(i, first, last):
                for t in range(4):
                    split_slots(slot_hi, st_conv.slot + RING + SPT * t, i * 16, SPT)
                    if first and t == 0:
                        root(STAT_H2, STAT_BANK)
                    if t == 2:
                        act.wait_ge(st_conv.taken, i * 4 + 3)
                        act.activation(tile_b[:, 0, :], tile_b[:, 0, :], ACT.Silu).then_inc(silu_done, 1)
                act.wait_ge(conv_ready, i + 1)
                act.activation(V_hi[:, i, :], tile_c[:, 0, :], ACT.Copy).then_inc(yc_hi, 1)

            loop(act, KT, conv_turn)
            for half in range(2):
                act.wait_ge(ple_a.stored[half], 16 * KT // 2)
            output(st_bout, out_b, ple_b, 1, h2_dram, U_hi)
            embed(ple_b, "e1", V["e1_raw"], SQ_E1)
            gated(st_ple1, ple_b, STAT_E1, 1, out, None)
            for half in range(2):
                act.wait_ge(ple_b.stored[half], 16 * KT // 2)

        @block.vector
        def _(dve):
            def add_square(at, row, first, parity):
                dve.wait_ge(squared, at + 1)
                if first:
                    dve.tensor_copy(total[:, row, :], squares[:, parity, :]).then_inc(summed, 1)
                else:
                    dve.wait_ge(summed, at)
                    dve.tensor_tensor(total[:, row, :], total[:, row, :], squares[:, parity, :], ALU.add).then_inc(
                        summed, 1)

            def invert(stat):
                r = rnorm[:, STAT_AT[stat], :]
                dve.wait_ge(root_done, stat + 1)
                dve.reciprocal(r, r).then_inc(rnorm_done, 1)
                dve.wait_ge(rnorm_done, stat + 1)

            def R(stat):
                return rnorm[:, STAT_AT[stat], :]

            x_raw = V["x_raw"]
            for k in range(KT):
                if k % KPS == 0:
                    split_slots(slot_lo, k // 2, 0, 2)
                for c, (a, b) in enumerate(X_CHUNKS):
                    if k == a:
                        dve.wait_ge(x_loaded[c], 16)
                if k == 0:
                    dve.wait_ge(cols_loaded, 16)
                dve.wait_ge(u_hi, k + 1)
                dve.scalar_tensor_tensor(U_lo[:, k, :], x_raw[:, k, :], col("norm0", k), f32(U_hi[:, k, :]),
                                         ALU.mult, ALU.subtract).then_inc(u_split, 1)
            for k in range(KT):
                add_square(SQ_X + k, 0, k == 0, k % 2)
                if k % KPS == KPS - 1:
                    split_slots(slot_lo, RING + k // 2 - 1, 0, 2)
            c_raw = V["c_raw"]

            def norm_c(n):
                if n >= 2:
                    dve.wait_ge(c_split, n - 1)
                dve.scalar_tensor_tensor(tile_b[:, n % 2, :], c_raw[:, n, :], col("kvg" if n < LT else "qg", n % LT),
                                         R(STAT_KV if n < LT else STAT_Q), ALU.mult, ALU.mult).then_inc(c_normed, 1)
                dve.wait_ge(c_hi_done, n + 1)
                dve.tensor_tensor(V["c_lo"][:, n, :], tile_b[:, n % 2, :], f32(V["c_hi"][:, n, :]),
                                  ALU.subtract).then_inc(c_split, 1)

            steps = [0]

            def step(ins):
                steps[0] += 1
                ins.then_inc(table_step, 1)
                dve.wait_ge(table_step, steps[0])

            def angles():
                two_pi = 2 * np.pi
                parts, rest = [], two_pi
                for bits in (5, 13, 21):
                    part = float(np.floor(rest * 2.0 ** bits) / 2.0 ** bits)
                    parts.append(part)
                    rest -= part
                parts.append(float(rest))
                magic = 1.5 * 2 ** 23
                n = TT * HALF
                dve.wait_ge(pos_loaded, 16)
                step(dve.tensor_copy(pos_f[:], pos_i[:]))
                ang = tile_c[:, 0, n:2 * n]
                for t in range(TT):
                    ins = dve.tensor_scalar(ang[:, t * HALF:(t + 1) * HALF], col("freq", 0, HALF), pos_f[:, t:t + 1], None,
                                            ALU.mult)
                step(ins)
                for s in range(2):
                    turns, r = tile_c[:, 1, n:2 * n], tile_c[:, s, 0:n]
                    step(dve.tensor_scalar(turns, ang, 1 / two_pi, 0.25 * s, ALU.mult, ALU.add))
                    step(dve.tensor_scalar(turns, turns, magic, None, ALU.add))
                    step(dve.tensor_scalar(turns, turns, -magic, None, ALU.add))
                    src = ang
                    for part in parts:
                        step(dve.scalar_tensor_tensor(r, turns, -part, src, ALU.mult, ALU.add))
                        src = r
                    step(dve.tensor_scalar(r, r, 0.5 * np.pi * s, 3.1415925, ALU.add, ALU.min))
                    dve.tensor_scalar(r, r, -3.1415925, None, ALU.max).then_inc(angles_ready, 1)

            def rotary_tables():
                dve.wait_ge(sines_ready, 2)
                sin, cos = tile_d[:, 0, 0:TT * HALF], tile_d[:, 1, 0:TT * HALF]
                for w, name in enumerate(("qrope", "krope")):
                    g1, g2 = col(name, 0, HALF), col(name, HALF, HALF)
                    for t in range(TT):
                        c, s = cos[:, t * HALF:(t + 1) * HALF], sin[:, t * HALF:(t + 1) * HALF]
                        dve.tensor_tensor(tables[:, w, 0, t, 0:HALF], c, g1, ALU.mult)
                        dve.tensor_tensor(tables[:, w, 0, t, HALF:], c, g2, ALU.mult)
                        dve.scalar_tensor_tensor(tables[:, w, 1, t, 0:HALF], s, -1.0, g2, ALU.mult, ALU.mult)
                        ins = dve.tensor_tensor(tables[:, w, 1, t, HALF:], s, g1, ALU.mult)
                ins.then_inc(tables_ready, 1)
                dve.wait_ge(tables_ready, 1)

            kr_tok = tile_a[:, 1, 0:TT * ROPE].rearrange("p (t f) -> p t f", t=TT)
            kr_tmp = tile_a[:, 1, TT * ROPE:].rearrange("p (t f) -> p t f", t=TT)

            def take_kr():
                dve.wait_ge(kr_turned, 1)
                halves = banks[:, KR_TURN_BANK, :].rearrange("p (t s f) -> p t s f", t=TT, s=2)
                step(dve.tensor_copy(kr_tmp, halves[:, :, 0, :]))
                step(dve.tensor_tensor(kr_tok, kr_tmp, halves[:, :, 1, :], ALU.add))
                step(dve.tensor_tensor(kr_tmp, kr_tok, kr_tok, ALU.mult))
                step(dve.tensor_reduce(ss_kr[:], kr_tmp, AX.X, ALU.add))

            def rotate_kr():
                step(dve.tensor_tensor(kr_tmp[:, :, 0:HALF], kr_tok[:, :, HALF:], tables[:, 1, 1, :, 0:HALF], ALU.mult))
                step(dve.tensor_tensor(kr_tmp[:, :, HALF:], kr_tok[:, :, 0:HALF], tables[:, 1, 1, :, HALF:], ALU.mult))
                step(dve.tensor_tensor(kr_tok, kr_tok, tables[:, 1, 0, :, :], ALU.mult))
                dve.tensor_tensor(kr_rot[:], kr_tok, kr_tmp, ALU.add).then_inc(kr_ready, 1)

            for n in range(2 * LT):
                if n > 1:
                    split_slots(slot_lo, st_c.slot + RING + SPT * n, 0, SPT)
                if n == 0:
                    invert(STAT_X)
                if n < 2:
                    dve.wait_ge(weights_used, RING)
                else:
                    tile_done(dve, st_c, 0, n)
                dve.tensor_tensor(c_raw[:, n, :], banks[:, n % 4, :], R(STAT_X), ALU.mult).then_inc(st_c.taken, 1)
                add_square(SQ_C + n, n // LT, n % LT == 0, n % 2)
                if n == LT - 1:
                    angles()
            split_slots(slot_lo, FIRST_SLOT["kr"] + RING, 0, RING)
            dve.wait_ge(weights_used, FIRST_SLOT["kr"] + RING)
            dve.tensor_tensor(tile_a[:, 0, :], banks[:, KR_BANK, :], R(STAT_X), ALU.mult).then_inc(kr_scaled, 1)

            def hook(t):
                if t == 0:
                    take_kr()
                    invert(STAT_KV)
                else:
                    if t == 1:
                        invert(STAT_Q)
                    for n in range(3 * t - 3, min(3 * t, 2 * LT)):
                        norm_c(n)
                if t == 3:
                    rotary_tables()
                    rotate_kr()

            def gate_turn(i, first, last):
                for t in range(4):
                    split_slots(slot_lo, st_gate.slot + RING + SPT * t, i * 16, SPT)
                    tile_done(dve, st_gate, i, t)
                    if not (first and t < 2):
                        dve.wait_ge(gate_saved[t % 2], i * 32 + 16 * (t // 2))
                    dve.tensor_tensor(gates[:, t % 2, :], banks[:, t, :], R(STAT_X), ALU.mult).then_inc(st_gate.taken, 1)
                    if first:
                        hook(t)

            loop(dve, KT // 4, gate_turn)

            v_hi, v_lo, pT_hi, pT_lo = S["v_hi"], S["v_lo"], S["pT_hi"], S["pT_lo"]
            kT_hi, kT_lo, qT_hi, qT_lo = V["kT_hi"], V["kT_lo"], V["qT_hi"], V["qT_lo"]
            swapped, k_rope = S["swapped"], S["k_rope"]
            q_tail = heads4[:, :, :, NOPE:]

            def k_variance(p):
                dve.wait_ge(proj_raw, p * 8 + 4)
                dve.tensor_tensor(ss_sum[:], ss_k[:], ss_kr[:].unsqueeze(2).to_broadcast([P, TT, 2]), ALU.add).then_inc(
                    ss_added, 1)
                dve.wait_ge(ss_added, p + 1)
                dve.tensor_scalar(var_k[:], ss_sum[:], 1.0 / QKH, EPS, ALU.mult, ALU.add).then_inc(var_k_ready, 1)

            def scale_keys(p):
                dve.wait_ge(rstd_k_ready, p + 1)
                r = rstd_k[:].unsqueeze(3)
                dve.tensor_tensor(keys4, keys4, r.to_broadcast([P, TT, 2, NOPE]), ALU.mult)
                dve.tensor_tensor(k_rope[:], kr_rot[:].unsqueeze(2).to_broadcast([P, TT, 2, ROPE]),
                                  r.to_broadcast([P, TT, 2, ROPE]), ALU.mult).then_inc(k_scaled, 1)

            def rotate_queries(p, part):
                tok, at = (slice(0, TT - 1) if part == 0 else slice(TT - 1, TT)), p * 4 + 2 * part
                n = tok.stop - tok.start
                tail, swap = q_tail[:, tok], swapped[:, tok]
                dve.wait_ge(proj_copied, p * 8 + (TT + tok.stop))
                for a, b in ((slice(0, HALF), slice(HALF, ROPE)), (slice(HALF, ROPE), slice(0, HALF))):
                    ins = dve.tensor_tensor(swap[:, :, :, a], tail[:, :, :, b],
                                            tables[:, 0, 1, tok, a].unsqueeze(2).to_broadcast([P, n, 2, HALF]), ALU.mult)
                ins.then_inc(rope_terms, 1)
                dve.wait_ge(rope_terms, at + 1)
                dve.tensor_tensor(tail, tail, tables[:, 0, 0, tok, :].unsqueeze(2).to_broadcast([P, n, 2, ROPE]),
                                  ALU.mult).then_inc(rope_terms, 1)
                dve.wait_ge(rope_terms, at + 2)
                dve.tensor_tensor(swap, swap, tail, ALU.add).then_inc(q_roped, 1)

            def query_variance(p):
                dve.wait_ge(proj_raw, p * 8 + 8)
                dve.tensor_scalar(var_q[:], ss_q[:], QKH * EPS, None, ALU.add).then_inc(var_q_ready, 1)

            def heads_rest(p, x):
                (of, row), gain = TURNS[x], TURN_GAIN[x]
                hi, lo = (kT_hi, kT_lo) if of == "k" else (qT_hi, qT_lo)
                dve.wait_ge(heads_hi, p * 6 + (x + 1))
                dve.scalar_tensor_tensor(lo[:, row, :], banks[:, TURN_BANK[x], :], col(gain) if gain else 1.0,
                                         f32(hi[:, row, :]), ALU.mult, ALU.subtract).then_inc(heads_split, 1)

            def peaks(p, h, late=False):
                scores = scores_of(late)
                if h == 0:
                    dve.wait_ge(scale_q_ready, p + 1)
                for n, group in enumerate(J_GROUPS):
                    dve.wait_ge(scores_done, p * 6 + (3 * h + n + 1))
                    for j in group:
                        ins = dve.tensor_reduce(peak[:, j:j + 1], scores[:, S_AT[j]:S_AT[j] + (j + 1) * P], AX.X, ALU.max)
                    ins.then_inc(peak_ready, 1)
                    dve.wait_ge(peak_ready, p * 6 + (3 * h + n + 1))
                    for j in group:
                        dve.scalar_tensor_tensor(shift[:, j:j + 1], peak[:, j:j + 1], -1.0, scale_q[:, j, h:h + 1],
                                                 ALU.mult, ALU.mult).then_inc(shift_ready, 1)

            def normalise(p, h, late=False):
                probs = probs_of(late)
                for n, j in enumerate(J_ORDER):
                    at = p * 8 + (4 * h + n + 1)
                    s = slice(S_AT[j], S_AT[j] + (j + 1) * P)
                    dve.wait_ge(exp_done, at)
                    dve.reciprocal(row_inv[:, j:j + 1], row_sum[:, j:j + 1]).then_inc(inv_ready, 1)
                    dve.wait_ge(inv_ready, at)
                    dve.tensor_scalar(probs[:, s], probs[:, s], row_inv[:, j:j + 1], None, ALU.mult).then_inc(
                        probs_ready, 1)

            def probs_rest(p, h, parts=(0, 1, 2), late=False):
                scores = scores_of(late)
                for n in parts:
                    a, b = PT_PARTS[n]
                    dve.wait_ge(pT_hi_done, p * 6 + (3 * h + n + 1))
                    dve.tensor_tensor(pT_lo[:, a:b], scores[:, a:b], f32(pT_hi[:, a:b]), ALU.subtract).then_inc(
                        pT_split, 1)

            def gate_head(p, h):
                dve.wait_ge(pv_done, p * 2 + (h + 1))
                dve.wait_ge(gate_loaded[h], p * 16 + 16)
                dve.tensor_tensor(gates[:, h, :], banks[:, O_BANK, :], gates[:, h, :], ALU.mult).then_inc(y_ready, 1)

            def attend(p, first, last):
                nxt = FIRST_SLOT["qkv"] + RING + 4
                peaks(p, 0)
                normalise(p, 0)
                if last:
                    peaks(p, 1, True)
                probs_rest(p, 0)
                if last:
                    normalise(p, 1, True)
                else:
                    split_slots(slot_lo, nxt, p * RING, 2)
                    k_variance(p + 1)
                    split_slots(slot_lo, nxt + 2, p * RING, 2)
                gate_head(p, 0)
                if not last:
                    scale_keys(p + 1)
                    slot_lo(nxt + 4, p * RING)
                if not last:
                    peaks(p, 1)
                    normalise(p, 1)
                    rotate_queries(p + 1, 0)
                    heads_rest(p + 1, 0)
                probs_rest(p, 1, (0,), last)
                if not last:
                    rotate_queries(p + 1, 1)
                    query_variance(p + 1)
                probs_rest(p, 1, (1, 2), last)
                if last:
                    split_slots(slot_lo, nxt, p * RING, 4)
                else:
                    for x in range(1, 6):
                        heads_rest(p + 1, x)
                    split_slots(slot_lo, nxt + 5, p * RING, 3)
                gate_head(p, 1)

            dve.wait_ge(kr_ready, 1)
            k_variance(0)
            scale_keys(0)
            rotate_queries(0, 0)
            heads_rest(0, 0)
            rotate_queries(0, 1)
            query_variance(0)
            for x in range(1, 6):
                heads_rest(0, x)
            split_slots(slot_lo, FIRST_SLOT["qkv"] + RING, 0, 4)
            loop(dve, PAIRS, attend)

            def output(st, o, ple, dst_hi, dst_lo):
                def turn(i, first, last):
                    for t in range(4):
                        n = i * 4 + t
                        if last and t < PLE_KT:
                            dve.wait_ge(ple.p_hi, t + 1)
                            dve.tensor_tensor(S["p_lo"][:, t, :], gates[:, t, :], f32(S["p_hi"][:, t, :]),
                                              ALU.subtract).then_inc(ple.p_split, 1)
                        split_slots(slot_lo, st.slot + RING + SPT * t, i * 16, SPT)
                        tile_done(dve, st, i, t)
                        dve.wait_ge(o.res_loaded[t % 2], i * 32 + 16 * (t // 2 + 1))
                        dve.tensor_tensor(tile_b[:, t % 2, :], banks[:, t, :], tile_a[:, t % 2, :], ALU.add).then_inc(
                            st.taken, 1)
                        dve.wait_ge(o.h_hi, n + 1)
                        dve.tensor_tensor(dst_lo[:, n, :], tile_b[:, t % 2, :], f32(dst_hi[:, n, :]),
                                          ALU.subtract).then_inc(o.h_split, 1)
                loop(dve, KT // 4, turn)

            def embed(ple, stage, sq0):
                for n in range(KT):
                    add_square(sq0 + n, 0, n == 0, n % 2)
                    if n % 2:
                        slot_lo(FIRST_SLOT[stage] + RING + n // 2)

            def gated(st, ple, stat, layer, h_hi, h_lo, e_raw, sq0):
                def turn(i, first, last):
                    for t in range(4):
                        n = i * 4 + t
                        half = t % 2
                        split_slots(slot_lo, st.slot + RING + SPT * t, i * 16, SPT)
                        if first and t == 0:
                            invert(stat)
                        dve.scalar_tensor_tensor(tile_b[:, half, :], e_raw[:, n, :], col(f"pleg{layer}", n), R(stat),
                                                 ALU.mult, ALU.mult).then_inc(ple.e_normed, 1)
                        dve.tensor_tensor(tile_c[:, half, :], f32(h_hi[:, n, :]), f32(h_lo[:, n, :]), ALU.add).then_inc(
                            ple.h_joined, 1)
                        dve.wait_ge(st.taken, n + 1)
                        dve.wait_ge(ple.e_normed, n + 1)
                        dve.tensor_tensor(tile_b[:, half, :], tile_a[:, half, :], tile_b[:, half, :], ALU.mult).then_inc(
                            ple.gated, 1)
                        dve.wait_ge(ple.gated, n + 1)
                        dve.wait_ge(ple.h_joined, n + 1)
                        if not (first and t < 2):
                            dve.wait_ge(ple.stored[half], i * 32 + 16 * (t // 2))
                            if layer == 0:
                                dve.wait_ge(squared, i * 4 + (sq0 + t - 1))
                        dve.tensor_tensor(tile_d[:, half, :], tile_b[:, half, :], tile_c[:, half, :], ALU.add).then_inc(
                            ple.h_ready, 1)
                        if layer == 0:
                            dve.wait_ge(ple.u_hi, n + 1)
                            dve.scalar_tensor_tensor(U_lo[:, n, :], tile_d[:, half, :], col("norm1", n),
                                                     f32(U_hi[:, n, :]), ALU.mult, ALU.subtract).then_inc(ple.u_split, 1)
                            add_square(i * 4 + (sq0 + t), 1, first and t == 0, half)
                loop(dve, KT // 4, turn)

            output(st_aout, out_a, ple_a, V_hi, V_lo)
            embed(ple_a, "e0", SQ_E0)
            gated(st_ple0, ple_a, STAT_E0, 0, V_hi, V_lo, U["e0_raw"], SQ_H2)

            conv_in = S["conv_in"]
            dve.memset(conv_in[:, 0:TAPS - 1], 0.0).then_inc(pad_zero, 1)
            taps = [tile_a[:, 0, :], tile_a[:, 1, :], tile_c[:, 1, :]]

            def conv_turn(i, first, last):
                r, r2 = R(STAT_H2), rnorm[:, R_SQUARE, :]
                for t in range(4):
                    split_slots(slot_lo, st_conv.slot + RING + SPT * t, i * 16, SPT)
                    if first and t == 0:
                        invert(STAT_H2)
                        dve.tensor_tensor(r2, r, r, ALU.mult).then_inc(rnorm_sq, 1)
                        dve.wait_ge(rnorm_sq, 1)
                        dve.wait_ge(pad_zero, 1)
                    tile_done(dve, st_conv, i, t)
                    ps = banks[:, t, :]
                    if t == 0:
                        dve.tensor_tensor(tile_a[:, 0, :], ps, r2, ALU.mult).then_inc(st_conv.taken, 1)
                    elif t == 1:
                        dve.wait_ge(st_conv.taken, i * 4 + 1)
                        dve.tensor_tensor(conv_in[:, TAPS - 1:], ps, tile_a[:, 0, :], ALU.mult).then_inc(
                            st_conv.taken, 1)
                        dve.wait_ge(st_conv.taken, i * 4 + 2)
                        dve.tensor_scalar(taps[1], conv_in[:, 2:], col("conv", i * TAPS + 2), None,
                                          ALU.mult).then_inc(tap_done, 1)
                        dve.wait_ge(tap_done, i * 3 + 1)
                        dve.scalar_tensor_tensor(taps[2], conv_in[:, 1:T + 1], col("conv", i * TAPS + 1), taps[1],
                                                 ALU.mult, ALU.add).then_inc(tap_done, 1)
                        dve.wait_ge(tap_done, i * 3 + 2)
                        dve.scalar_tensor_tensor(taps[1], conv_in[:, 0:T], col("conv", i * TAPS), taps[2],
                                                 ALU.mult, ALU.add).then_inc(tap_done, 1)
                    elif t == 2:
                        dve.tensor_tensor(tile_b[:, 0, :], ps, r, ALU.mult).then_inc(st_conv.taken, 1)
                    else:
                        dve.tensor_tensor(tile_b[:, 1, :], ps, r, ALU.mult).then_inc(st_conv.taken, 1)
                        dve.wait_ge(silu_done, i + 1)
                        dve.wait_ge(tap_done, i * 3 + 3)
                        dve.tensor_tensor(taps[2], tile_b[:, 0, :], taps[1], ALU.mult).then_inc(conv_part, 1)
                        dve.wait_ge(conv_part, i + 1)
                        dve.wait_ge(st_conv.taken, i * 4 + 4)
                        dve.tensor_tensor(tile_c[:, 0, :], tile_b[:, 1, :], taps[2], ALU.mult).then_inc(conv_ready, 1)
                dve.wait_ge(yc_hi, i + 1)
                dve.tensor_tensor(V_lo[:, i, :], tile_c[:, 0, :], f32(V_hi[:, i, :]), ALU.subtract).then_inc(yc_split, 1)

            loop(dve, KT, conv_turn)
            output(st_bout, out_b, ple_b, U_hi, U_lo)
            embed(ple_b, "e1", SQ_E1)
            gated(st_ple1, ple_b, STAT_E1, 1, U_hi, U_lo, V["e1_raw"], None)


def _tiles(w):
    k, n = w.shape
    return np.ascontiguousarray(
        w.reshape(k // SLOT, KPS, P, n // P, P).transpose(3, 0, 2, 1, 4).reshape(-1, P, SLOT))


def _columns(v, width=P):
    return v.reshape(-1, width).T


def _layout(a):
    w_in = a["a_w_in"][0]
    c_q, c_kv, k_r, gate = np.split(w_in, [LORA, 2 * LORA, 2 * LORA + ROPE], axis=1)
    arrays = {}
    w_c = _tiles(np.concatenate([c_kv, c_q], axis=1))
    pair = w_c[:RING].reshape(2, SPT, P, SLOT).transpose(1, 0, 2, 3)
    arrays["w_c"] = np.concatenate([pair.reshape(RING, P, SLOT), w_c[RING:]])
    per = KT // RING
    arrays["w_kr"] = k_r.reshape(RING, per, P, ROPE).transpose(0, 2, 1, 3).reshape(RING, P, per * ROPE)
    arrays["w_gate"] = _tiles(gate)
    kv = a["a_w_kv_up"][0].reshape(LT, P, PAIRS, 2, 2, P).transpose(2, 0, 1, 4, 3, 5).reshape(PAIRS, LT, P, 512)
    q = a["a_w_q_up"][0].reshape(LT, P, PAIRS, QW).transpose(2, 0, 1, 3)
    q = np.concatenate([q, q[..., :SLOT - QW]], axis=3)
    arrays["w_qkv"] = np.concatenate([kv, q], axis=1).reshape(PAIRS * RING, P, SLOT)
    arrays["w_aout"] = _tiles(a["a_w_out"][0])
    arrays["w_ple0"], arrays["w_ple1"] = (_tiles(a["ple_w_gate"][i]) for i in range(2))
    for i in range(2):
        e = a["ple_w_proj"][i].reshape(PLE_KT, P, RING, 2, P).transpose(2, 1, 3, 0, 4)
        arrays[f"w_e{i}"] = e.reshape(RING, P, SLOT)
    parts = a["b_w_in"][0].reshape(D, 4, KT, P)
    parts = np.stack([parts[:, s] for s in (1, 2, 3, 0)], axis=2)
    arrays["w_conv"] = _tiles(parts.reshape(D, 4 * D))
    arrays["w_bout"] = _tiles(a["b_w_out"][0])
    arrays["x"] = a["x"][0].T.reshape(KT, P, T)
    arrays["p"] = a["p"][:, 0].transpose(0, 2, 1).reshape(2, PLE_KT, P, T)
    arrays["pos"] = a["positions"][0].reshape(TT, P).T
    conv = a["b_conv_w"][0].reshape(TAPS, KT, P).transpose(2, 1, 0).reshape(P, KT * TAPS)
    freq = (np.float32(THETA) ** (-np.arange(0, ROPE, 2, dtype=np.float32) / np.float32(ROPE))).astype(np.float32)

    def spread(v):
        return np.broadcast_to(v[None, :], (P, v.size))

    arrays["cols"] = np.concatenate([
        _columns(a["norm_g"][0]), _columns(a["norm_g"][1]), _columns(a["a_kv_norm_g"][0]), _columns(a["a_q_norm_g"][0]),
        _columns(a["a_qn_g"][0][:NOPE]), _columns(a["a_kn_g"][0][:NOPE]), _columns(a["ple_norm_g"][0]),
        _columns(a["ple_norm_g"][1]), _columns(a["ple_b_gate"][0]), _columns(a["ple_b_gate"][1]), conv,
        spread(a["a_qn_g"][0][NOPE:]), spread(a["a_kn_g"][0][NOPE:]), spread(freq)], axis=1)
    return {k: np.ascontiguousarray(v) for k, v in arrays.items()}


def kernel(**inputs):
    import concourse.bacc as bacc
    from concourse.bass_utils import run_bass_kernel_spmd

    arrays = _layout({k: np.asarray(v) for k, v in inputs.items()})
    nc = bacc.Bacc("TRN2", target_bir_lowering=False, num_devices=1, dynamic_dma_scratch_size=1024)
    A = {k: nc.dram_tensor("in_" + k, v.shape, mybir.dt.from_np(v.dtype), kind="ExternalInput").ap() for k, v in arrays.items()}
    out = nc.dram_tensor("out", [KT, P, T], F32, kind="ExternalOutput").ap()
    build(nc, A, out)
    result = run_bass_kernel_spmd(nc, [{"in_" + k: v for k, v in arrays.items()}], core_ids=[0])
    return np.ascontiguousarray(result.results[0]["out"].reshape(D, T).T)[None]
```
